# Optimizing a Trainium2 kernel written in Bass

```python
import math
import jax, jax.numpy as jnp
from jax import lax
import numpy as np

D_MODEL = 2048
BATCH = 1
SEQ = 256
DEPTH = 1

N_MEM = 256
D_MIX = D_MODEL
D_CONV = 3 * D_MIX // 8
D_POOL = 3 * D_MIX // 8
D_XATT = D_MIX // 4
CONV_HEAD_DIM = 128
CONV_HEADS = D_CONV // CONV_HEAD_DIM
CONV_WIDTH = 3
POOL_WINDOWS = (2, 4, 8, 16)
POOL_GROUPS = len(POOL_WINDOWS)
POOL_GROUP_DIM = D_POOL // POOL_GROUPS
XATT_HEADS = 4
XATT_HEAD_DIM = D_XATT // XATT_HEADS
D_FF = ((8 * D_MODEL // 3 + 255) // 256) * 256
FFN_CONV_WIDTH = 3
D_IN = 3 * D_CONV + D_POOL + D_XATT
EPS = 1e-6


def rmsnorm(x, g):
    xf = x.astype(jnp.float32)
    y = xf * lax.rsqrt(jnp.mean(xf * xf, axis=-1, keepdims=True) + EPS)
    return (y * g.astype(jnp.float32)).astype(x.dtype)

def causal_dwconv(u, w):
    k = w.shape[0]
    s = u.shape[1]
    up = jnp.pad(u, ((0, 0), (k - 1, 0), (0, 0)))
    out = w[k - 1] * u
    for j in range(k - 1):
        out = out + w[j] * up[:, j:j + s]
    return out

def causal_pool_minus_self(v):
    s = v.shape[1]
    vf = v.astype(jnp.float32)
    c = jnp.pad(jnp.cumsum(vf, axis=1), ((0, 0), (1, 0), (0, 0), (0, 0)))
    t = jnp.arange(s, dtype=jnp.float32)[None, :, None]
    outs = []
    for g, k in enumerate(POOL_WINDOWS):
        cg = c[:, :, g]
        hi = cg[:, 1:]
        lo = jnp.pad(cg[:, :s + 1 - k], ((0, 0), (k - 1, 0), (0, 0)))
        cnt = jnp.minimum(t + 1.0, float(k))
        outs.append((hi - lo) / cnt - vf[:, :, g])
    return jnp.stack(outs, axis=2).astype(v.dtype)

def first_inputs(seed: int = 0) -> dict:
    key = jax.random.key(seed)
    ks = jax.random.split(key, 18)
    f32 = jnp.float32
    nrm = lambda k, shape, scale: (jax.random.normal(k, shape, f32) * scale)
    gain = lambda k, shape: 1.0 + 0.05 * jax.random.normal(k, shape, f32)
    L = DEPTH
    return {
        "x": jax.random.normal(ks[0], (BATCH, SEQ, D_MODEL), f32),
        "mem": jax.random.normal(ks[1], (BATCH, N_MEM, D_MODEL), f32),
        "g_mix": gain(ks[2], (L, D_MODEL)),
        "g_mem": gain(ks[3], (L, D_MODEL)),
        "w_in": nrm(ks[4], (L, D_MODEL, D_IN), D_MODEL ** -0.5),
        "conv_w": nrm(ks[5], (L, CONV_WIDTH, D_CONV), CONV_WIDTH ** -0.5),
        "pool_w": nrm(ks[6], (L, POOL_GROUPS, POOL_GROUP_DIM, POOL_GROUP_DIM), POOL_GROUP_DIM ** -0.5),
        "pool_scale": gain(ks[7], (L, D_POOL)),
        "w_kv": nrm(ks[8], (L, D_MODEL, 2 * D_XATT), D_MODEL ** -0.5),
        "w_out": nrm(ks[9], (L, D_MIX, D_MODEL), D_MIX ** -0.5),
        "g_ffn": gain(ks[10], (L, D_MODEL)),
        "w_up": nrm(ks[11], (L, D_MODEL, 2 * D_FF), D_MODEL ** -0.5),
        "ffn_conv_w": nrm(ks[12], (L, FFN_CONV_WIDTH, 2 * D_FF), FFN_CONV_WIDTH ** -0.5),
        "ffn_conv_b": nrm(ks[13], (L, 2 * D_FF), 0.01),
        "w_down": nrm(ks[14], (L, D_FF, D_MODEL), D_FF ** -0.5),
        "g_final": gain(ks[15], (D_MODEL,)),
    }

def first_block(x, mem, g_mix, g_mem, w_in, conv_w, pool_w, pool_scale, w_kv, w_out,
              g_ffn, w_up, ffn_conv_w, ffn_conv_b, w_down, g_final):
    b, s, _ = x.shape
    split_pts = [D_CONV, 2 * D_CONV, 3 * D_CONV, 3 * D_CONV + D_POOL]
    att_scale = 1.0 / math.sqrt(XATT_HEAD_DIM)
    for l in range(DEPTH):
        h = rmsnorm(x, g_mix[l])
        z = h @ w_in[l]
        cb, cc, cx, pv, q = jnp.split(z, split_pts, axis=-1)

        conv_out = cb * causal_dwconv(cc * cx, conv_w[l])

        pooled = causal_pool_minus_self(pv.reshape(b, s, POOL_GROUPS, POOL_GROUP_DIM))
        pool_out = jnp.einsum('bsgc,gcd->bsgd', pooled, pool_w[l]).reshape(b, s, D_POOL)
        pool_out = pool_out * pool_scale[l]

        m = rmsnorm(mem, g_mem[l])
        kv = m @ w_kv[l]
        k, v = jnp.split(kv, 2, axis=-1)
        k = k.reshape(b, N_MEM, XATT_HEADS, XATT_HEAD_DIM)
        v = v.reshape(b, N_MEM, XATT_HEADS, XATT_HEAD_DIM)
        qh = q.reshape(b, s, XATT_HEADS, XATT_HEAD_DIM)
        scores = jnp.einsum('bshd,bmhd->bhsm', qh, k).astype(jnp.float32) * att_scale
        probs = jax.nn.softmax(scores, axis=-1).astype(x.dtype)
        att = jnp.einsum('bhsm,bmhd->bshd', probs, v).reshape(b, s, D_XATT)

        mix = jnp.concatenate([conv_out, pool_out, att], axis=-1)
        x = x + mix @ w_out[l]

        h = rmsnorm(x, g_ffn[l])
        u = causal_dwconv(h @ w_up[l], ffn_conv_w[l]) + ffn_conv_b[l]
        gate, val = jnp.split(u, 2, axis=-1)
        x = x + (jax.nn.silu(gate) * val) @ w_down[l]
    return rmsnorm(x, g_final)


HEAD_DIM = 128
MIX_WIDTH = D_MODEL
A_HEADS = MIX_WIDTH // (2 * HEAD_DIM)
B_HEADS = MIX_WIDTH // (2 * HEAD_DIM)
A_WIDTH = A_HEADS * HEAD_DIM
B_WIDTH = B_HEADS * HEAD_DIM
DIFF_DIM = HEAD_DIM // 2
IN_WIDTH = 3 * A_WIDTH + 3 * B_WIDTH
DILATED_CONFIGS = ((128, 1), (512, 4), (2048, 16))
ROPE_THETA = 500000.0
ROPE_FRACTION = 4
D_FF_2 = ((-(-8 * D_MODEL // 3) + 255) // 256) * 256
Q_BLOCK = 128
RMS_EPS = 1e-6
SUBLN_EPS = 1e-5
NEG_INF = -1e30


def rmsnorm_2(x, g, eps=RMS_EPS):
    xf = x.astype(jnp.float32)
    y = xf * lax.rsqrt(jnp.mean(xf * xf, axis=-1, keepdims=True) + eps)
    return (y * g.astype(jnp.float32)).astype(x.dtype)

def rope_tables(seq, rot_dim):
    inv_freq = ROPE_THETA ** (-jnp.arange(0, rot_dim, 2, dtype=jnp.float32) / rot_dim)
    ang = jnp.arange(seq, dtype=jnp.float32)[:, None] * inv_freq[None, :]
    return jnp.cos(ang), jnp.sin(ang)

def rope(x, cos, sin):
    r2 = cos.shape[-1]
    shape = (x.shape[1],) + (1,) * (x.ndim - 3) + (r2,)
    c, s = cos.reshape(shape), sin.reshape(shape)
    x1, x2 = x[..., :r2], x[..., r2:2 * r2]
    return jnp.concatenate([x1 * c - x2 * s, x2 * c + x1 * s, x[..., 2 * r2:]], axis=-1).astype(x.dtype)

def dilated_branch(q, k, v, dil, half):
    B, S, H, Dh = q.shape
    L = S // dil
    nb = -(-L // half)
    Lp = nb * half

    def by_residue(a):
        return a.reshape(B, L, dil, H, Dh).transpose(0, 2, 3, 1, 4)

    qs = jnp.pad(by_residue(q), ((0, 0), (0, 0), (0, 0), (0, Lp - L), (0, 0))).reshape(B, dil, H, nb, half, Dh)
    kpad = ((0, 0), (0, 0), (0, 0), (half, Lp - L + half), (0, 0))
    kp = jnp.pad(by_residue(k), kpad).reshape(B, dil, H, nb + 2, half, Dh)
    vp = jnp.pad(by_residue(v), kpad).reshape(B, dil, H, nb + 2, half, Dh)

    def band(a):
        return jnp.concatenate([a[:, :, :, :-2], a[:, :, :, 1:-1], a[:, :, :, 2:]], axis=4)

    kb, vb = band(kp), band(vp)
    s = jnp.einsum('brhnqe,brhnke->brhnqk', qs, kb, preferred_element_type=jnp.float32) * (Dh ** -0.5)
    blk = jnp.arange(nb)[:, None, None]
    qa = jnp.arange(half)[None, :, None]
    kj = jnp.arange(3 * half)[None, None, :]
    kpos = blk * half - half + kj
    dist = kj - half - qa
    mask = (jnp.abs(dist) <= half) & (kpos >= 0) & (kpos < L)
    s = jnp.where(mask, s, NEG_INF)
    m = jnp.max(s, axis=-1, keepdims=True)
    p = jnp.exp(s - m)
    den = jnp.sum(p, axis=-1)
    o = jnp.einsum('brhnqk,brhnke->brhnqe', p, vb.astype(jnp.float32)) / den[..., None]
    lse = m[..., 0] + jnp.log(den)
    o = o.reshape(B, dil, H, Lp, Dh)[:, :, :, :L].transpose(0, 3, 1, 2, 4).reshape(B, S, H, Dh)
    lse = lse.reshape(B, dil, H, Lp)[:, :, :, :L].transpose(0, 3, 1, 2).reshape(B, S, H)
    return o, lse

def dilated_attention(q, k, v):
    outs, lses = [], []
    for window, dil in DILATED_CONFIGS:
        o, lse = dilated_branch(q, k, v, dil, window // (2 * dil))
        outs.append(o)
        lses.append(lse)
    w = jax.nn.softmax(jnp.stack(lses, axis=0), axis=0)
    return jnp.einsum('gbsh,gbshe->bshe', w, jnp.stack(outs, axis=0))

def diff_attention(q, k, v, lam):
    B, S, H, _, d = q.shape
    nqb = S // Q_BLOCK
    qb = q.reshape(B, nqb, Q_BLOCK, H, 2, d).transpose(1, 0, 3, 4, 2, 5)
    kt = k.transpose(0, 2, 3, 1, 4)
    vt = v.transpose(0, 2, 1, 3)

    def one_block(qblk):
        s = jnp.einsum('bhcqe,bhcke->bhcqk', qblk, kt, preferred_element_type=jnp.float32) * (d ** -0.5)
        p = jax.nn.softmax(s, axis=-1)
        a = p[:, :, 0] - lam * p[:, :, 1]
        return jnp.einsum('bhqk,bhke->bhqe', a, vt.astype(jnp.float32))

    o = lax.map(one_block, qb)
    return o.transpose(1, 0, 3, 2, 4).reshape(B, S, H, 2 * d)

def second_inputs(seed: int = 0) -> dict:
    key = jax.random.key(seed)
    ks = jax.random.split(key, 11)
    f32 = jnp.float32

    def dense(k, shape):
        return jax.random.normal(k, shape, f32) * (shape[-2] ** -0.5)

    def gain(k, shape):
        return 1.0 + 0.02 * jax.random.normal(k, shape, f32)

    return {
        'x': jax.random.normal(ks[0], (BATCH, SEQ, D_MODEL), f32),
        'norm_attn': gain(ks[1], (DEPTH, D_MODEL)),
        'w_in': dense(ks[2], (DEPTH, D_MODEL, IN_WIDTH)),
        'lambda_qk': 0.1 * jax.random.normal(ks[3], (DEPTH, 4, DIFF_DIM), f32),
        'subln': gain(ks[4], (DEPTH, 2 * DIFF_DIM)),
        'w_out': dense(ks[5], (DEPTH, MIX_WIDTH, D_MODEL)),
        'norm_ffn': gain(ks[6], (DEPTH, D_MODEL)),
        'w_gate': dense(ks[7], (DEPTH, D_MODEL, D_FF_2)),
        'w_up': dense(ks[8], (DEPTH, D_MODEL, D_FF_2)),
        'w_down': dense(ks[9], (DEPTH, D_FF_2, D_MODEL)),
        'norm_final': gain(ks[10], (D_MODEL,)),
    }

def second_block(x, norm_attn, w_in, lambda_qk, subln, w_out, norm_ffn, w_gate, w_up, w_down, norm_final):
    B, S, _ = x.shape
    cos_a, sin_a = rope_tables(S, HEAD_DIM // ROPE_FRACTION)
    cos_b, sin_b = rope_tables(S, DIFF_DIM // ROPE_FRACTION)
    splits = [A_WIDTH, 2 * A_WIDTH, 3 * A_WIDTH, 3 * A_WIDTH + B_WIDTH, 3 * A_WIDTH + 2 * B_WIDTH]
    for l in range(DEPTH):
        h = rmsnorm_2(x, norm_attn[l])
        proj = h @ w_in[l]
        qa, ka, va, qb, kb, vb = jnp.split(proj, splits, axis=-1)
        qa = rope(qa.reshape(B, S, A_HEADS, HEAD_DIM), cos_a, sin_a)
        ka = rope(ka.reshape(B, S, A_HEADS, HEAD_DIM), cos_a, sin_a)
        va = va.reshape(B, S, A_HEADS, HEAD_DIM)
        ya = dilated_attention(qa, ka, va).astype(x.dtype).reshape(B, S, A_WIDTH)
        lam_init = 0.8 - 0.6 * math.exp(-0.3 * l)
        lq = lambda_qk[l].astype(jnp.float32)
        lam = jnp.exp(jnp.sum(lq[0] * lq[1])) - jnp.exp(jnp.sum(lq[2] * lq[3])) + lam_init
        qb = rope(qb.reshape(B, S, B_HEADS, 2, DIFF_DIM), cos_b, sin_b)
        kb = rope(kb.reshape(B, S, B_HEADS, 2, DIFF_DIM), cos_b, sin_b)
        vb = vb.reshape(B, S, B_HEADS, 2 * DIFF_DIM)
        yb = diff_attention(qb, kb, vb, lam)
        yb = (rmsnorm_2(yb, subln[l], SUBLN_EPS) * (1.0 - lam_init)).astype(x.dtype).reshape(B, S, B_WIDTH)
        x = x + jnp.concatenate([ya, yb], axis=-1) @ w_out[l]
        h = rmsnorm_2(x, norm_ffn[l])
        x = x + (jax.nn.silu(h @ w_gate[l]) * (h @ w_up[l])) @ w_down[l]
    return rmsnorm_2(x, norm_final)


def setup_inputs(seed=0):
    out = dict(first_inputs(seed))
    for name, value in second_inputs(seed + 1).items():
        if name != "x":
            out[name + "_2"] = value
    return out


def reference(
    x, mem, g_mix, g_mem, w_in, conv_w, pool_w, pool_scale, w_kv, w_out, g_ffn, w_up,
    ffn_conv_w, ffn_conv_b, w_down, g_final, norm_attn_2, w_in_2, lambda_qk_2, subln_2, w_out_2,
    norm_ffn_2, w_gate_2, w_up_2, w_down_2, norm_final_2,
):
    x = first_block(
        x, mem, g_mix, g_mem, w_in, conv_w, pool_w, pool_scale, w_kv, w_out, g_ffn, w_up,
        ffn_conv_w, ffn_conv_b, w_down, g_final,
    )
    return second_block(
        x, norm_attn_2, w_in_2, lambda_qk_2, subln_2, w_out_2, norm_ffn_2, w_gate_2, w_up_2,
        w_down_2, norm_final_2,
    )


_drawn_inputs = setup_inputs


def setup_inputs(seed=0):
    import zlib

    import numpy as np

    out = dict(_drawn_inputs(seed))
    spreads = {}
    factors = {'g_mem': 8.0,
     'ffn_conv_b': 5.265,
     'norm_attn_2': 2.68,
     'subln_2': 5.867,
     'norm_ffn_2': 4.275,
     'norm_final_2': 2.761}
    for name, (base, spread) in spreads.items():
        noise = np.random.default_rng([zlib.crc32(name.encode()), seed]).standard_normal(out[name].shape)
        drawn = base * np.exp(spread * noise) if base else spread * noise
        out[name] = __import__('jax').numpy.asarray(drawn.astype(out[name].dtype))
    for name, factor in factors.items():
        out[name] = (out[name] * factor).astype(out[name].dtype)
    return out
```

```python
import math
from contextlib import ExitStack

import numpy as np
import concourse.bass as bass
from concourse import mybir

F32, F32R = mybir.dt.float32, mybir.dt.float32r
ACT, ALU, AX = mybir.ActivationFunctionType, mybir.AluOpType, mybir.AxisListType

P = 128
S = 256
D = 2048
KT = D // P
FF = 5632
FT = FF // P
N_HEADS_X = 4
N_HEADS_A = 8
N_HEADS_B = 8
RING = 4
CHUNK_K = 4
PAIR = 2 * P
LOOKAHEAD = 3
WINDOWS = (2, 4, 8, 16)
GROUP = 192
PAD = max(WINDOWS)
ROT_A, ROT_B = 32, 16
LAM_INIT = 0.8 - 0.6 * math.exp(-0.3 * 0)
EPS, SUBLN_EPS = 1e-6, 1e-5
Z_CB, Z_CC, Z_CX, Z_PV, Z_Q, Z_K, Z_V = 0, 6, 12, 18, 24, 28, 32
Z_INVCNT, Z_POOLW = 36, 40
POOL_BLOCKS = [(h, a, b) for h in range(2) for b in range(3) for a in range(3) if abs(a - b) < 2]
POOL_PARTS = [[(0, 128, 0)], [(0, 64, 0), (64, 128, 1)], [(0, 128, 1)],
              [(0, 128, 2)], [(0, 64, 2), (64, 128, 3)], [(0, 128, 3)]]


class Phase:

    def __init__(self, name, k_tiles, pairs, kind):
        self.name, self.k_tiles, self.pairs, self.kind = name, k_tiles, pairs, kind
        self.chunks = k_tiles // CHUNK_K


def phases():
    out = [Phase("kv", KT, 4, "z"), Phase("in1", KT, 14, "z"), Phase("out1", KT, 8, "res"),
           Phase("up1", KT, 44, "ffn"), Phase("down1", FT, 8, "res2"), Phase("in2", KT, 24, "z"),
           Phase("out2", KT, 8, "res"), Phase("up2", KT, 44, "glu"), Phase("down2", FT, 8, "last")]
    chunk = pair = 0
    res, glu = KT, 0
    slot = [0] * RING
    for n, ph in enumerate(out):
        ph.index = n
        ph.chunk0, ph.pair0, ph.slot0 = chunk, pair, list(slot)
        ph.res0, ph.glu0 = res, glu
        ph.slot_uses = [len(range(s, ph.chunks, RING)) for s in range(RING)]
        chunk += ph.pairs * ph.chunks
        pair += ph.pairs
        slot = [a + ph.pairs * b for a, b in zip(slot, ph.slot_uses)]
        res += ph.pairs if ph.kind in ("res", "res2", "last") else 0
        glu += ph.pairs // 2 if ph.kind in ("ffn", "glu") else 0
    return out


class Chain:

    def __init__(self):
        self.base, self.local, self.start = 0, 0, 0

    def step(self):
        self.local += 1
        return self.base + self.local

    def now(self):
        return self.base + self.local

    def enter(self, i, first, per):
        self.start = self.base + self.local
        self.base, self.local = self.start + (i - first) * per, 0

    def leave(self, first, end, per):
        assert self.local == per, (self.local, per)
        self.base, self.local = self.start + (end - first) * per, 0


def build(nc, xT, memT, w_kv, w_in, w_out, w_up, w_down, w_in_2, w_out_2, w_up_2, w_gate_2, w_down_2,
          gains, conv_w, pool_w, pool_scale, ffn_conv_w, ffn_conv_b, lambda_qk, subln,
          ident_c, logc_c, ropea_c, ropeb_c, invcnt_c, outT):
    PH = phases()
    by_name = {ph.name: ph for ph in PH}
    ctx = ExitStack()
    with ctx:
        def sem(name):
            return ctx.enter_context(nc.semaphore(name))

        def sb(name, shape, dt=F32):
            return ctx.enter_context(nc.sbuf_tensor(name, shape, dt))

        raw = sb("raw", [P, RING, CHUNK_K, PAIR])
        w_hi = sb("w_hi", [P, RING, CHUNK_K, PAIR], F32R)
        w_lo = sb("w_lo", [P, RING, CHUNK_K, PAIR], F32R)
        xs = sb("xs", [P, KT, 2, S], F32R)
        x = sb("x", [P, KT, S])
        ident = sb("ident", [P, P])
        ones = sb("ones", [P, P])
        logc = sb("logc", [P, 2, S])
        ropea = sb("ropea", [ROT_A, 2, S])
        ropeb = sb("ropeb", [P, 2, S])
        gain = sb("gain", [P, 8, KT])
        cw = sb("cw", [P, 3, 6])
        pscale = sb("pscale", [P, 6])
        fcw = sb("fcw", [P, 3, 2 * FT])
        fcb = sb("fcb", [P, 2 * FT])
        sg = sb("sg", [P, 1])
        eps = sb("eps", [P, 2])
        neg_max = sb("neg_max", [P, 2, 4])
        den = sb("den", [P, 2, 4])
        rden = sb("rden", [P, 4])
        lam = sb("lam", [P, 4, 64])
        lam_sum = sb("lam_sum", [P, 2])
        neg_lam = sb("neg_lam", [P, 1])
        r = sb("r", [P, S])
        rt = sb("rt", [P, S])
        ssum = sb("ssum", [P, 2, S])
        sq = sb("sq", [P, 2, S])
        ssum_g = sb("ssum_g", [P, 2, S])
        sq_g = sb("sq_g", [P, 2, S])
        r_x = sb("r_x", [P, S])
        u = sb("u", [P, 2, 2 + S])
        a_gate = sb("a_gate", [P, 2, S])
        a_val = sb("a_val", [P, 2, S])
        silu = sb("silu", [P, 2, S])
        with ExitStack() as mixer:
            z = mixer.enter_context(nc.sbuf_tensor("z", [P, 48, S], F32))
            mixs = mixer.enter_context(nc.sbuf_tensor("mixs", [P, KT, 2, S], F32R))
            sc = mixer.enter_context(nc.sbuf_tensor("sc", [P, 2, 2, 2, S], F32))
        acts = sb("acts", [P, FT, 2, S], F32R)
        proj = ctx.enter_context(nc.psum_tensor("proj", [P, 4, 512], F32))
        misc = ctx.enter_context(nc.psum_tensor("misc", [P, 4, 512], F32))

        invcnt = z[:, Z_INVCNT:Z_INVCNT + 4, :]
        poolw = z[:, Z_POOLW:Z_POOLW + 7, :].rearrange("p a (b n) -> p (a b) n", n=P)
        levels = sc[:].rearrange("p a b c s -> p (a b c s)")[:, 0:5 * (PAD + S)].rearrange("p (l n) -> p l n", l=5)
        r_mem = silu[:, 0, :]
        pT, v_sb, y_sb, ysq = a_gate, a_val[:].rearrange("p b (m d) -> p b m d", d=P), silu[:, 0, :], silu[:, 1, :]
        scores, probs_t, o_ps = misc[:, 0:2, :].rearrange("p c (t s) -> p c t s", t=2), misc[:, 2, :].rearrange("p (m s) -> p m s", m=2), misc[:, 3, 0:S]
        v_ps, head_stat = proj[:, 0, 0:S], proj[:, 1, 0:S]
        stat, stat_g = misc[:, 0, 0:S], misc[:, 1, 0:S]

        mem_loaded = [sem(f"mem_loaded{n}") for n in range(4)]
        x_loaded = [sem(f"x_loaded{n}") for n in range(4)]
        gain_loaded, tables_loaded = sem("gain_loaded"), sem("tables_loaded")
        raw_loaded = [sem(f"raw_loaded{n}") for n in range(RING)]
        out_stored = sem("out_stored")
        hi_ready, lo_ready, chunk_used, bank_free = sem("hi_ready"), sem("lo_ready"), sem("chunk_used"), sem("bank_free")
        xs_ready, mixs_ready, acts_ready = sem("xs_ready"), sem("mixs_ready"), sem("acts_ready")
        res_hi_ready, ssum_ready, stat_done, root_ready = sem("res_hi_ready"), sem("ssum_ready"), sem("stat_done"), sem("root_ready")
        consts_ready, vector_step = sem("consts_ready"), sem("vector_step")
        tap2_ready, taps_ready, silu_ready, prod_ready, act_hi_ready = sem("tap2_ready"), sem("taps_ready"), sem("silu_ready"), sem("prod_ready"), sem("act_hi_ready")
        conv_g_ready, conv_tap_ready, conv_p_ready, conv_hi_ready = sem("conv_g_ready"), sem("conv_tap_ready"), sem("conv_p_ready"), sem("conv_hi_ready")
        poolw_zeroed, poolw_loaded, pooled_ready, pool_mm_done, pool_hi_ready = sem("poolw_zeroed"), sem("poolw_loaded"), sem("pooled_ready"), sem("pool_mm_done"), sem("pool_hi_ready")
        lam_ready, lam_exp_ready, lam_loaded = sem("lam_ready"), sem("lam_exp_ready"), sem("lam_loaded")
        roped, mean_g_ready = sem("roped"), sem("mean_g_ready")
        v_turned, v_copied, scored, scores_read, max_ready, exp_ready, probs_ready = sem("v_turned"), sem("v_copied"), sem("scored"), sem("scores_read"), sem("max_ready"), sem("exp_ready"), sem("probs_ready")
        probs_turned, probs_copied, attended, att_sq_ready, att_stat_done, att_root_ready, att_y_ready, att_hi_ready = sem("probs_turned"), sem("probs_copied"), sem("attended"), sem("att_sq_ready"), sem("att_stat_done"), sem("att_root_ready"), sem("att_y_ready"), sem("att_hi_ready")

        moving = {"kv": mixs, "in1": xs, "out1": mixs, "up1": xs, "down1": acts, "in2": xs, "out2": mixs, "up2": xs, "down2": acts}
        z_base = {"kv": Z_K, "in1": 0, "in2": 0}
        gain_row = {"x": 0, "mem": 1, "out1": 2, "out2": 5, "down1": 7}
        N_BLOCK, N_FINAL = 3, 6
        MIX1 = 3 + 3 + N_HEADS_X
        MIX2 = N_HEADS_A + N_HEADS_B
        inputs = {"kv": (mixs_ready, 0, 2), "in1": (xs_ready, 0, 2), "out1": (mixs_ready, 8 + MIX1, 0),
                  "up1": (xs_ready, 8, 2), "down1": (acts_ready, 0, 2), "in2": (xs_ready, 16, 2),
                  "out2": (mixs_ready, 8 + MIX1 + MIX2, 0), "up2": (xs_ready, 24, 2), "down2": (acts_ready, FT // 2, 2)}

        def weight_columns(ph, i, a):
            if ph.name == "up1":
                return w_up, a * FF + PAIR * i
            if ph.name == "up2":
                return (w_gate_2, w_up_2)[a], PAIR * i
            w = {"kv": w_kv, "in1": w_in, "out1": w_out, "down1": w_down, "in2": w_in_2, "out2": w_out_2, "down2": w_down_2}[ph.name]
            return w, PAIR * (2 * i + a)

        units1 = [(h, (Z_Q + h, Z_K + h, Z_V + h, 1, 12 + h, None, 8 + 6 + h)) for h in range(N_HEADS_X)]
        base2 = 8 + MIX1
        units2 = [(N_HEADS_X + h, (h, 8 + h, 16 + h, 1, h, None, base2 + h)) for h in range(N_HEADS_A)]
        units2 += [(N_HEADS_X + N_HEADS_A + h, (24 + h, 32 + h, 40 + h, 2, 8 + h, h, base2 + N_HEADS_A + h)) for h in range(N_HEADS_B)]

        POOLW_LOADS = 16 * (1 + sum(max(a * P, g * GROUP) < min((a + 1) * P, (g + 1) * GROUP) and
                                    max(b * P, g * GROUP) < min((b + 1) * P, (g + 1) * GROUP)
                                    for _, a, b in POOL_BLOCKS for g in range(2)))

        norms = ["kv", "in1", "up1", "in2", "up2"]
        NORMS = len(norms) + 1

        def q_is(i, a, q):
            return isinstance(i, int) and 2 * i + a == q

        def final_pair(ph, i, a):
            return isinstance(i, int) and 2 * i + a == ph.pairs - 1

        def chunk_index(ph, q, c):
            return ph.chunk0 + q * ph.chunks + c

        def wait_slot(eng, ph, q, c, semaphore):
            back = LOOKAHEAD if c < LOOKAHEAD else RING
            n = chunk_index(ph, q, c) - back + 1
            if not isinstance(n, int) or n > 0:
                eng.wait_ge(semaphore, n)

        def ahead(ph, q, c):
            if c + LOOKAHEAD < ph.chunks:
                return q, c + LOOKAHEAD
            if ph is PH[-1] and isinstance(q, int) and q == ph.pairs - 1:
                return None
            return q + 1, c + LOOKAHEAD - ph.chunks

        block = ctx.enter_context(nc.Block())

        @block.gpsimd
        def _(pool):
            nc.gpsimd.memset(z[:, Z_POOLW:Z_POOLW + 7, :], 0.0).then_inc(poolw_zeroed, 1)
            pool.wait_ge(poolw_zeroed, 1)
            pool.dma_start(invcnt, invcnt_c).then_inc(poolw_loaded, 16)
            for n, (h, a, b) in enumerate(POOL_BLOCKS):
                for g in range(2):
                    r0, r1 = max(a * P, g * GROUP), min((a + 1) * P, (g + 1) * GROUP)
                    c0, c1 = max(b * P, g * GROUP), min((b + 1) * P, (g + 1) * GROUP)
                    if r0 < r1 and c0 < c1:
                        pool.dma_start(poolw[r0 - a * P:r1 - a * P, n, c0 - b * P:c1 - b * P],
                                       pool_w[2 * h + g, r0 - g * GROUP:r1 - g * GROUP, c0 - g * GROUP:c1 - g * GROUP],
                                       ).then_inc(poolw_loaded, 16)
        tables = [(gain[:], gains), (ident[:], ident_c), (cw[:], conv_w), (pscale[:], pool_scale), (fcw[:], ffn_conv_w),
                  (fcb[:], ffn_conv_b), (sg[:], subln), (logc[:], logc_c), (ropea[:], ropea_c), (ropeb[:], ropeb_c)]

        @block.sync
        def _(sp):
            sp.dma_start(gain[:, 0:7, :], gains).then_inc(gain_loaded, 16)
            for n in range(4):
                sp.dma_start(z[:, 4 * n:4 * n + 4, :], memT[512 * n:512 * n + 512, :].rearrange("(k p) s -> p k s", p=P)).then_inc(mem_loaded[n], 16)

            def load_pair(ph, i, a):
                w, col = weight_columns(ph, i, a)
                q = 2 * i + a
                for c in range(ph.chunks):
                    wait_slot(sp, ph, q, c, lo_ready)
                    sp.dma_start(raw[:, c % RING, :, :],
                                 w[512 * c:512 * c + 512, bass.ds(col, PAIR)].rearrange("(k p) n -> p k n", p=P)
                                 ).then_inc(raw_loaded[c % RING], 16)

            for ph in PH:
                if ph.name == "kv":
                    load_pair(ph, 0, 0)
                    for n in range(4):
                        sp.dma_start(x[:, 4 * n:4 * n + 4, :], xT[512 * n:512 * n + 512, :].rearrange("(k p) s -> p k s", p=P)).then_inc(x_loaded[n], 16)
                    for dst, src in tables[1:]:
                        sp.dma_start(dst, src).then_inc(tables_loaded, 16)
                    sp.dma_start(lam[:], lambda_qk.partition_broadcast(P)).then_inc(lam_loaded, 16)
                    load_pair(ph, 0, 1)
                    for i in range(1, ph.pairs // 2):
                        load_pair(ph, i, 0)
                        load_pair(ph, i, 1)
                else:
                    with sp.Fori(0, ph.pairs // 2) as i:
                        load_pair(ph, i, 0)
                        load_pair(ph, i, 1)
            for n in range(4):
                sp.wait_ge(xs_ready, (KT // 2) * (NORMS - 2) + n + 1)
                sp.dma_start(outT[512 * n:512 * n + 512, :].rearrange("(k p) s -> p k s", p=P), x[:, 4 * n:4 * n + 4, :]).then_inc(out_stored, 16)
            sp.wait_ge(out_stored, 64)

        @block.tensor
        def _(pe):
            def project_pair(ph, i, a, first=False):
                q, mv = 2 * i + a, moving[ph.name]
                for c in range(ph.chunks):
                    s = c % RING
                    pe.wait_ge(lo_ready, chunk_index(ph, q, c) + 1)
                    if first:
                        ready, before, each = inputs[ph.name]
                        pe.wait_ge(ready, before + each * (c + 1))
                    if c == 0 and not (isinstance(q, int) and ph.pair0 + q < 2):
                        pe.wait_ge(bank_free, ph.pair0 + q - 1)
                    for j in range(2):
                        out = proj[:, 2 * a + j, 0:S]
                        for kk in range(CHUNK_K):
                            k = CHUNK_K * c + kk
                            hi, lo = w_hi[:, s, kk, P * j:P * j + P], w_lo[:, s, kk, P * j:P * j + P]
                            nc.tensor.matmul(out, hi, mv[:, k, 0, :], start=(k == 0), stop=False)
                            nc.tensor.matmul(out, hi, mv[:, k, 1, :], start=False, stop=False)
                            last = nc.tensor.matmul(out, lo, mv[:, k, 0, :], start=False, stop=(k == ph.k_tiles - 1))
                    last.then_inc(chunk_used, 1)

            def token_sums(n, sums, sums_g=None):
                pe.wait_ge(ssum_ready, n)
                for out, s in ((stat, sums), (stat_g, sums_g)):
                    if s is not None:
                        nc.tensor.matmul(out, ones[:], s[:, 0, :], start=True, stop=False)
                        last = nc.tensor.matmul(out, ones[:], s[:, 1, :], start=False, stop=True)
                last.then_inc(stat_done, 1)

            def pool_products():
                pe.wait_ge(poolw_loaded, POOLW_LOADS)
                for t in range(6):
                    h, b = divmod(t, 3)
                    blocks = [(n, a) for n, (hh, a, bb) in enumerate(POOL_BLOCKS) if (hh, bb) == (h, b)]
                    pe.wait_ge(pooled_ready, 6)
                    out = misc[:, t // 2, S * (t % 2):S * (t % 2) + S]
                    for m, (n, a) in enumerate(blocks):
                        last = nc.tensor.matmul(out, poolw[:, n, :], z[:, Z_PV + 3 * h + a, :], start=(m == 0), stop=(m == len(blocks) - 1))
                    if t % 2:
                        last.then_inc(pool_mm_done, 1)

            def turn_v_and_score(n, unit):
                q, k, v, comps = unit[:4]
                if n >= 1:
                    pe.wait_ge(v_copied, n)
                for m in range(2):
                    last = nc.tensor.transpose(v_ps[:, P * m:P * m + P], z[:, v, P * m:P * m + P], ident[:])
                last.then_inc(v_turned, 1)
                if n >= 1:
                    pe.wait_ge(scores_read, n)
                rows = P // comps
                for c in range(comps):
                    for t in range(2):
                        last = nc.tensor.matmul(scores[:, c, t, :], z[rows * c:rows * c + rows, q, P * t:P * t + P],
                                                z[rows * c:rows * c + rows, k, :], start=True, stop=True)
                last.then_inc(scored, 1)

            def attend(n, unit):
                pe.wait_ge(probs_ready, n + 1)
                if n >= 1:
                    pe.wait_ge(probs_copied, n)
                for m in range(2):
                    for t in range(2):
                        last = nc.tensor.transpose(probs_t[:, m, P * t:P * t + P], sc[:, n % 2, 0, t, P * m:P * m + P], ident[:])
                last.then_inc(probs_turned, 1)
                pe.wait_ge(v_copied, n + 1)
                pe.wait_ge(probs_copied, n + 1)
                if n >= 1:
                    pe.wait_ge(mixs_ready, unit[6])
                for m in range(2):
                    last = nc.tensor.matmul(o_ps, v_sb[:, n % 2, m, :], pT[:, m, :], start=(m == 0), stop=(m == 1))
                last.then_inc(attended, 1)

            def head_sums(unit):
                pe.wait_ge(att_sq_ready, unit[5] + 1)
                if unit[5]:
                    pe.wait_ge(att_root_ready, unit[5])
                nc.tensor.matmul(head_stat, ones[:], ysq, start=True, stop=True).then_inc(att_stat_done, 1)

            def attention(units):
                turn_v_and_score(*units[0])
                for m, (n, unit) in enumerate(units):
                    if m + 1 < len(units):
                        turn_v_and_score(*units[m + 1])
                    attend(n, unit)
                    if unit[5] is not None:
                        head_sums(unit)

            pe.wait_ge(consts_ready, 1)
            for ph in PH:
                if ph.name == "out1":
                    pe.wait_ge(tables_loaded, 16 * (len(tables) - 1))
                    pool_products()
                    pe.wait_ge(pool_hi_ready, 3)
                    pe.wait_ge(mixs_ready, 8 + 6)
                    attention(units1)
                if ph.name == "out2":
                    pe.wait_ge(roped, 8)
                    attention(units2)
                project_pair(ph, 0, 0, first=True)
                if ph.name in norms:
                    token_sums(norms.index(ph.name) + 1, a_gate if ph.name == "kv" else ssum,
                               ssum_g if ph.name == "in2" else None)
                project_pair(ph, 0, 1)
                with pe.Fori(1, ph.pairs // 2) as i:
                    project_pair(ph, i, 0)
                    project_pair(ph, i, 1)
            token_sums(NORMS, ssum)

        @block.scalar
        def _(act):
            def split_hi(ph, i, a, c):
                if (at := ahead(ph, 2 * i + a, c)) is None:
                    return
                q, c = at
                s = c % RING
                act.wait_ge(raw_loaded[s], 16 * (ph.slot0[s] + q * ph.slot_uses[s] + c // RING + 1))
                wait_slot(act, ph, q, c, chunk_used)
                nc.scalar.activation(w_hi[:, s, :, :], raw[:, s, :, :], ACT.Copy).then_inc(hi_ready, 1)

            def norm_input(src, tile, dst, row):
                nc.scalar.activation(sq[:], src, ACT.Square)
                for j in range(2):
                    last = nc.scalar.activation(dst[:, bass.ds(tile + j, 1), 0, :], src[:, j:j + 1, :], ACT.Copy,
                                                scale=gain[:, row, bass.ds(tile + j, 1)])
                last.then_inc(res_hi_ready, 1)

            def prepare(n, src, loaded, dst, row, sq_free):
                act.wait_ge(loaded[n // 2], 16)
                if sq_free is not None:
                    act.wait_ge(*sq_free)
                norm_input(src[:, 2 * n:2 * n + 2, :], 2 * n, dst, row)

            def root(n):
                act.wait_ge(stat_done, n)
                nc.scalar.activation(rt[:], stat, ACT.Sqrt, bias=eps[:, 0:1], scale=1.0 / D).then_inc(root_ready, 1)

            def leave(stage, ph, i, a):
                q = 2 * i + a
                if stage == 0 and q_is(i, a, 0) and ph.name in norms:
                    root(norms.index(ph.name) + 1)
                    if ph.name == "in2":
                        act.wait_ge(mean_g_ready, 1)
                        nc.scalar.activation(rt[:], sq_g[:, 0, :], ACT.Sqrt, bias=eps[:, 0:1], scale=1.0 / D).then_inc(root_ready, 1)
                if stage == 0 and ph.kind in ("res", "res2", "last"):
                    act.wait_ge(bank_free, ph.pair0 + q + 1)
                    if ph.kind == "res2":
                        for j in range(2):
                            nc.scalar.activation(sq_g[:, j:j + 1, :], x[:, bass.ds(2 * q + j, 1), :], ACT.Square,
                                                 scale=gain[:, N_BLOCK, bass.ds(2 * q + j, 1)])
                    if ph.kind != "last":
                        norm_input(x[:, bass.ds(2 * q, 2), :], 2 * q, xs, gain_row[ph.name])
                    else:
                        nc.scalar.activation(sq[:], x[:, bass.ds(2 * q, 2), :], ACT.Square).then_inc(res_hi_ready, 1)
                if ph.kind == "ffn" and stage == 0:
                    act.wait_ge(bank_free, ph.pair0 + q + 1)
                    dst = (a_gate, a_val)[a]
                    for j in range(2):
                        t = a * FT + 2 * i + j
                        last = nc.scalar.activation(dst[:, j, :], u[:, j, 2:2 + S], ACT.Identity,
                                                    bias=fcb[:, bass.ds(t, 1)], scale=fcw[:, 2, bass.ds(t, 1)])
                    last.then_inc(tap2_ready, 1)
                if ph.kind in ("ffn", "glu") and a == 0 and stage == 2:
                    if ph.kind == "ffn":
                        act.wait_ge(taps_ready, q + 2)
                    else:
                        act.wait_ge(bank_free, ph.pair0 + q + 1)
                    nc.scalar.activation(silu[:], a_gate[:], ACT.Silu).then_inc(silu_ready, 1)
                if ph.kind in ("ffn", "glu") and a == 1 and stage == 3:
                    act.wait_ge(prod_ready, ph.glu0 + i + 1)
                    nc.scalar.activation(acts[:, bass.ds(2 * i, 2), 0, :], a_val[:], ACT.Copy).then_inc(act_hi_ready, 1)

            def conv_pair(t):
                act.wait_ge(conv_g_ready, t + 1)
                for j in range(2):
                    last = nc.scalar.activation(a_gate[:, j, :], u[:, j, 2:2 + S], ACT.Copy, scale=cw[:, 2, 2 * t + j:2 * t + j + 1])
                last.then_inc(conv_tap_ready, 1)
                act.wait_ge(conv_p_ready, t + 1)
                nc.scalar.activation(mixs[:, Z_CB + 2 * t:Z_CB + 2 * t + 2, 0, :], a_gate[:], ACT.Copy).then_inc(conv_hi_ready, 1)

            def pool_out():
                for m in range(3):
                    act.wait_ge(pool_mm_done, m + 1)
                    for j in range(2):
                        t = 2 * m + j
                        last = nc.scalar.activation(mixs[:, 6 + t, 0, :], misc[:, m, S * j:S * j + S], ACT.Copy, scale=pscale[:, t:t + 1])
                    last.then_inc(pool_hi_ready, 1)

            def copy_v(n):
                act.wait_ge(v_turned, n + 1)
                nc.scalar.activation(v_sb[:, n % 2], v_ps.rearrange("p (m d) -> p m d", m=2), ACT.Copy).then_inc(v_copied, 1)

            def exps(n, unit):
                b, comps = n % 2, unit[3]
                act.wait_ge(max_ready, n + 1)
                for c in range(comps):
                    for t in range(2):
                        m = 2 * c + t
                        last = nc.scalar.activation(sc[:, b, c, t, :], sc[:, b, c, t, :], ACT.Exp, bias=neg_max[:, b, m:m + 1],
                                                    scale=1.0, accum_out=den[:, b, m:m + 1])
                last.then_inc(exp_ready, 1)

            def copy_probs(n):
                act.wait_ge(probs_turned, n + 1)
                nc.scalar.activation(pT[:], probs_t, ACT.Copy).then_inc(probs_copied, 1)

            def head_out(n, unit):
                act.wait_ge(attended, n + 1)
                if unit[5] is None:
                    nc.scalar.activation(mixs[:, unit[4], 0, :], o_ps, ACT.Copy).then_inc(att_hi_ready, 1)
                    return
                nc.scalar.activation(y_sb, o_ps, ACT.Copy)
                nc.scalar.activation(ysq, o_ps, ACT.Square).then_inc(att_sq_ready, 1)
                act.wait_ge(att_stat_done, unit[5] + 1)
                nc.scalar.activation(rt[:], head_stat, ACT.Sqrt, bias=eps[:, 1:2], scale=1.0 / P).then_inc(att_root_ready, 1)

            def head_hi(n, unit):
                if unit[5] is not None:
                    act.wait_ge(att_y_ready, unit[5] + 1)
                    nc.scalar.activation(mixs[:, unit[4], 0, :], y_sb, ACT.Copy).then_inc(att_hi_ready, 1)

            def attention(units):
                copy_v(units[0][0])
                for m, (n, unit) in enumerate(units):
                    exps(n, unit)
                    if m + 1 < len(units):
                        copy_v(n + 1)
                    if m:
                        head_hi(*units[m - 1])
                    copy_probs(n)
                    head_out(n, unit)
                head_hi(*units[-1])

            kv = by_name["kv"]
            act.wait_ge(gain_loaded, 16)
            act.wait_ge(consts_ready, 1)
            for c in range(-LOOKAHEAD, 0):
                split_hi(kv, 0, 0, c)
                for n in (2 * (c + LOOKAHEAD), 2 * (c + LOOKAHEAD) + 1):
                    prepare(n, z, mem_loaded, mixs, gain_row["mem"], (mixs_ready, n) if n else None)
            for n in (6, 7):
                prepare(n, z, mem_loaded, mixs, gain_row["mem"], (mixs_ready, n))

            def slot(ph, i, a, before):
                for c in range(ph.chunks):
                    if before is not None and c < 4:
                        leave(c, *before)
                    if ph.name == "kv" and c in (1, 2):
                        n = 2 * (2 * i + a) + c - 1
                        prepare(n, x, x_loaded, xs, gain_row["x"], (xs_ready, n) if n else (mixs_ready, 8))
                    split_hi(ph, i, a, c)

            before = None
            for ph in PH:
                last_i = ph.pairs // 2 - 1
                if ph.name in ("out1", "out2"):
                    for stage in range(4):
                        leave(stage, *before)
                    before = None
                if ph.name == "out1":
                    act.wait_ge(tables_loaded, 16 * (len(tables) - 1))
                    for t in range(3):
                        conv_pair(t)
                    pool_out()
                    attention(units1)
                if ph.name == "out2":
                    act.wait_ge(lam_ready, 1)
                    nc.scalar.activation(lam_sum[:], lam_sum[:], ACT.Exp).then_inc(lam_exp_ready, 1)
                    attention(units2)
                slot(ph, 0, 0, before)
                if ph.name == "kv":
                    for i in range(last_i):
                        slot(ph, i, 1, (ph, i, 0))
                        slot(ph, i + 1, 0, (ph, i, 1))
                else:
                    slot(ph, 0, 1, (ph, 0, 0))
                    slot(ph, 1, 0, (ph, 0, 1))
                    with act.Fori(1, last_i) as i:
                        slot(ph, i, 1, (ph, i, 0))
                        slot(ph, i + 1, 0, (ph, i, 1))
                slot(ph, last_i, 1, (ph, last_i, 0))
                before = (ph, last_i, 1)
            leave(0, *before)
            root(NORMS)

        @block.vector
        def _(dve):
            chain = Chain()

            def step(ins):
                ins.then_inc(vector_step, 1)
                dve.wait_ge(vector_step, chain.step())

            def over(t, n, rows=P):
                return t[0:rows, :].unsqueeze(1).broadcast_to([rows, n, S])

            def split_lo(ph, i, a, c):
                if (at := ahead(ph, 2 * i + a, c)) is None:
                    return
                q, c = at
                dve.wait_ge(hi_ready, chunk_index(ph, q, c) + 1)
                s = c % RING
                nc.vector.tensor_tensor(w_lo[:, s, :, :], raw[:, s, :, :], w_hi[:, s, :, :].bitcast(F32), ALU.subtract).then_inc(lo_ready, 1)

            def add_squares(sums, final, both=False):
                ins = nc.vector.tensor_tensor(sums[:], sums[:], sq[:], ALU.add)
                if both:
                    step(ins)
                    ins = nc.vector.tensor_tensor(ssum_g[:], ssum_g[:], sq_g[:], ALU.add)
                if final:
                    ins.then_inc(ssum_ready, 1)
                else:
                    step(ins)

            def norm_input_lo(n, src, tile, dst, row, sums, ready, final, both=False):
                dve.wait_ge(res_hi_ready, n + 1)
                add_squares(sums, final, both)
                for j in range(2):
                    last = nc.vector.scalar_tensor_tensor(
                        dst[:, bass.ds(tile + j, 1), 1, :], src[:, j:j + 1, :], gain[:, row, bass.ds(tile + j, 1)],
                        dst[:, bass.ds(tile + j, 1), 0, :].bitcast(F32), ALU.mult, ALU.subtract)
                last.then_inc(ready, 1)

            def reciprocal_root(n, dst):
                dve.wait_ge(root_ready, n)
                step(nc.vector.reciprocal(dst, rt[:]))

            def root_number(ph):
                return norms.index(ph.name) + 1 + (ph.name == "up2")

            def norm_of_norm():
                reciprocal_root(norms.index("in2") + 1, r_x[:])
                step(nc.vector.tensor_tensor(sq_g[:, 0, :], stat_g, r_x[:], ALU.mult))
                nc.vector.tensor_tensor(sq_g[:, 0, :], sq_g[:, 0, :], r_x[:], ALU.mult).then_inc(mean_g_ready, 1)
                reciprocal_root(norms.index("in2") + 2, r[:])
                step(nc.vector.tensor_tensor(r[:], r[:], r_x[:], ALU.mult))

            def scale_x(pair):
                for j in range(2):
                    last = nc.vector.scalar_tensor_tensor(x[:, bass.ds(2 * pair + j, 1), :], x[:, bass.ds(2 * pair + j, 1), :],
                                                          gain[:, N_BLOCK, bass.ds(2 * pair + j, 1)], over(r_x, 1), ALU.mult, ALU.mult)
                step(last)

            def leave(stage, ph, i, a):
                q = 2 * i + a
                banks = proj[:, 2 * a:2 * a + 2, 0:S]
                if stage == 0:
                    if q_is(i, a, 0) and ph.name == "in2":
                        norm_of_norm()
                    elif q_is(i, a, 0) and ph.name in norms:
                        reciprocal_root(root_number(ph), r_mem if ph.name == "kv" else r[:])
                    dve.wait_ge(chunk_used, chunk_index(ph, q + 1, 0))
                    if ph.kind == "z":
                        nc.vector.tensor_tensor(z[:, bass.ds(z_base[ph.name] + 2 * q, 2), :], banks,
                                                over(r_mem if ph.name == "kv" else r, 2), ALU.mult).then_inc(bank_free, 1)
                    if ph.kind in ("res", "res2", "last"):
                        nc.vector.tensor_tensor(x[:, bass.ds(2 * q, 2), :], banks, x[:, bass.ds(2 * q, 2), :], ALU.add).then_inc(bank_free, 1)
                    if ph.kind == "ffn":
                        dve.wait_ge(taps_ready, q + 1)
                        nc.vector.tensor_tensor(u[:, :, 2:2 + S], banks, over(r, 2), ALU.mult).then_inc(bank_free, 1)
                    if ph.kind == "glu":
                        if a == 1:
                            dve.wait_ge(acts_ready, ph.glu0 + i)
                        nc.vector.tensor_tensor((a_gate, a_val)[a][:], banks, over(r, 2), ALU.mult).then_inc(bank_free, 1)
                if stage == 1 and ph.kind in ("res", "res2"):
                    norm_input_lo(ph.res0 + q, x[:, bass.ds(2 * q, 2), :], 2 * q, xs, gain_row[ph.name], ssum, xs_ready, final_pair(ph, i, a), ph.kind == "res2")
                if stage == 1 and ph.kind == "last":
                    dve.wait_ge(res_hi_ready, ph.res0 + q + 1)
                    add_squares(ssum, final_pair(ph, i, a))
                if stage == 1 and ph.kind == "ffn":
                    dst = (a_gate, a_val)[a]
                    dve.wait_ge(tap2_ready, q + 1)
                    for tap in (1, 0):
                        for j in range(2):
                            last = nc.vector.scalar_tensor_tensor(dst[:, j, :], u[:, j, tap:tap + S], fcw[:, tap, bass.ds(a * FT + 2 * i + j, 1)],
                                                                  dst[:, j, :], ALU.mult, ALU.add)
                        if tap:
                            step(last)
                    last.then_inc(taps_ready, 1)
                if stage == 2 and a == 1 and ph.kind in ("ffn", "glu"):
                    dve.wait_ge(silu_ready, ph.glu0 + i + 1)
                    if ph.kind == "ffn":
                        dve.wait_ge(taps_ready, q + 2)
                    else:
                        dve.wait_ge(bank_free, ph.pair0 + q + 1)
                    nc.vector.tensor_tensor(a_val[:], silu[:], a_val[:], ALU.mult).then_inc(prod_ready, 1)
                if stage == 3 and a == 1 and ph.kind in ("ffn", "glu"):
                    dve.wait_ge(act_hi_ready, ph.glu0 + i + 1)
                    nc.vector.tensor_tensor(acts[:, bass.ds(2 * i, 2), 1, :], a_val[:], acts[:, bass.ds(2 * i, 2), 0, :].bitcast(F32),
                                            ALU.subtract).then_inc(acts_ready, 1)

            def conv_pair(t):
                nc.vector.tensor_tensor(u[:, :, 2:2 + S], z[:, Z_CC + 2 * t:Z_CC + 2 * t + 2, :], z[:, Z_CX + 2 * t:Z_CX + 2 * t + 2, :],
                                        ALU.mult).then_inc(conv_g_ready, 1)
                dve.wait_ge(conv_tap_ready, t + 1)
                for tap in (1, 0):
                    for j in range(2):
                        last = nc.vector.scalar_tensor_tensor(a_gate[:, j, :], u[:, j, tap:tap + S], cw[:, tap, 2 * t + j:2 * t + j + 1],
                                                              a_gate[:, j, :], ALU.mult, ALU.add)
                    step(last)
                nc.vector.tensor_tensor(a_gate[:], a_gate[:], z[:, Z_CB + 2 * t:Z_CB + 2 * t + 2, :], ALU.mult).then_inc(conv_p_ready, 1)
                dve.wait_ge(conv_hi_ready, t + 1)
                nc.vector.tensor_tensor(mixs[:, 2 * t:2 * t + 2, 1, :], a_gate[:], mixs[:, 2 * t:2 * t + 2, 0, :].bitcast(F32),
                                        ALU.subtract).then_inc(mixs_ready, 1)

            def pool_tile(t):
                v = z[:, Z_PV + t, :]
                step(nc.vector.tensor_copy(levels[:, 0, PAD:], v))
                for w in range(max(p[2] for p in POOL_PARTS[t]) + 1):
                    step(nc.vector.tensor_tensor(levels[:, w + 1, PAD:], levels[:, w, PAD:], levels[:, w, PAD - 2 ** w:PAD + S - 2 ** w], ALU.add))
                for p0, p1, w in POOL_PARTS[t]:
                    last = nc.vector.tensor_tensor(levels[p0:p1, w + 1, PAD:], levels[p0:p1, w + 1, PAD:], invcnt[p0:p1, w, :], ALU.mult)
                step(last)
                for p0, p1, w in POOL_PARTS[t]:
                    last = nc.vector.tensor_tensor(z[p0:p1, Z_PV + t, :], levels[p0:p1, w + 1, PAD:], z[p0:p1, Z_PV + t, :], ALU.subtract)
                last.then_inc(pooled_ready, 1)
                dve.wait_ge(pooled_ready, t + 1)

            def pool_out():
                for m in range(3):
                    dve.wait_ge(pool_hi_ready, m + 1)
                    for j in range(2):
                        t = 2 * m + j
                        last = nc.vector.scalar_tensor_tensor(mixs[:, 6 + t, 1, :], misc[:, m, S * j:S * j + S], pscale[:, t:t + 1],
                                                              mixs[:, 6 + t, 0, :].bitcast(F32), ALU.mult, ALU.subtract)
                    last.then_inc(mixs_ready, 1)

            def rope_group(n, tiles, rows, table, half):
                zt, turned = z[0:rows, tiles:tiles + 4, :], sc[0:rows, 0].rearrange("p c t s -> p (c t) s")
                step(nc.vector.stream_shuffle(turned, zt, [k + half if k < half else k - half if k < 2 * half else k for k in range(32)]))
                step(nc.vector.tensor_tensor(turned, turned, over(table[:, 1, :], 4, rows), ALU.mult))
                step(nc.vector.tensor_tensor(zt, zt, over(table[:, 0, :], 4, rows), ALU.mult))
                nc.vector.tensor_tensor(zt, zt, turned, ALU.add).then_inc(roped, 1)
                dve.wait_ge(roped, n + 1)

            def maxima(n, unit):
                b, comps = n % 2, unit[3]
                masked = N_HEADS_X <= n < N_HEADS_X + N_HEADS_A
                scale = (P // comps) ** -0.5
                dve.wait_ge(scored, n + 1)
                if n >= 2:
                    dve.wait_ge(probs_turned, n - 1)
                for c in range(comps):
                    if masked:
                        last = nc.vector.scalar_tensor_tensor(sc[:, b, c], scores[:, c], scale, logc[:], ALU.mult, ALU.add)
                    else:
                        last = nc.vector.tensor_scalar(sc[:, b, c], scores[:, c], scale, None, ALU.mult)
                last.then_inc(scores_read, 1)
                dve.wait_ge(scores_read, n + 1)
                for c in range(comps):
                    last = nc.vector.reduce_max(neg_max[:, b, 2 * c:2 * c + 2], sc[:, b, c], AX.X, negate=True)
                last.then_inc(max_ready, 1)

            def normalise(n, unit):
                b, comps = n % 2, unit[3]
                dve.wait_ge(exp_ready, n + 1)
                step(nc.vector.reciprocal(rden[:, 0:2 * comps], den[:, b, 0:2 * comps]))
                if comps == 2:
                    step(nc.vector.tensor_scalar(rden[:, 2:4], rden[:, 2:4], neg_lam[:, 0:1], None, ALU.mult))
                for t in range(2):
                    last = nc.vector.tensor_scalar(sc[:, b, 0, t, :], sc[:, b, 0, t, :], rden[:, t:t + 1], None, ALU.mult)
                if comps == 2:
                    step(last)
                    for t in range(2):
                        last = nc.vector.scalar_tensor_tensor(sc[:, b, 0, t, :], sc[:, b, 1, t, :], rden[:, 2 + t:3 + t], sc[:, b, 0, t, :],
                                                              ALU.mult, ALU.add)
                last.then_inc(probs_ready, 1)

            def head_lo(n, unit):
                src = o_ps
                if unit[5] is not None:
                    dve.wait_ge(att_root_ready, unit[5] + 1)
                    step(nc.vector.reciprocal(r_x[:], rt[:]))
                    nc.vector.scalar_tensor_tensor(y_sb, y_sb, sg[:, 0:1], r_x[:], ALU.mult, ALU.mult).then_inc(att_y_ready, 1)
                    src = y_sb
                dve.wait_ge(att_hi_ready, n + 1)
                nc.vector.tensor_tensor(mixs[:, unit[4], 1, :], src, mixs[:, unit[4], 0, :].bitcast(F32), ALU.subtract).then_inc(mixs_ready, 1)

            def attention(units):
                maxima(*units[0])
                for m, (n, unit) in enumerate(units):
                    if m + 1 < len(units):
                        maxima(*units[m + 1])
                    normalise(n, unit)
                    if m:
                        head_lo(*units[m - 1])
                head_lo(*units[-1])

            nc.vector.memset(ones[:], 1.0)
            nc.vector.memset(eps[:, 0:1], EPS)
            nc.vector.memset(eps[:, 1:2], SUBLN_EPS)
            nc.vector.memset(u[:, :, 0:2], 0.0).then_inc(taps_ready, 1)
            step(nc.vector.memset(ssum[:], 0.0))
            nc.vector.memset(a_gate[:], 0.0).then_inc(consts_ready, 1)
            dve.wait_ge(consts_ready, 1)
            dve.wait_ge(gain_loaded, 16)
            step(nc.vector.tensor_tensor(gain[:, 7, :], gain[:, N_BLOCK, :], gain[:, 4, :], ALU.mult))
            kv = by_name["kv"]

            def prepare_mem(n):
                norm_input_lo(n, z[:, 2 * n:2 * n + 2, :], 2 * n, mixs, gain_row["mem"], a_gate, mixs_ready, n == KT // 2 - 1)

            for c in range(-LOOKAHEAD, 0):
                split_lo(kv, 0, 0, c)
                for n in (2 * (c + LOOKAHEAD), 2 * (c + LOOKAHEAD) + 1):
                    prepare_mem(n)
            for n in (6, 7):
                prepare_mem(n)

            def slot(ph, i, a, before):
                for c in range(ph.chunks):
                    if before is not None and c < 4:
                        leave(c, *before)
                    if ph.name == "kv" and c in (1, 2):
                        n = 2 * (2 * i + a) + c - 1
                        norm_input_lo(KT // 2 + n, x[:, 2 * n:2 * n + 2, :], 2 * n, xs, gain_row["x"], ssum, xs_ready, n == KT // 2 - 1)
                    split_lo(ph, i, a, c)

            before = None
            for ph in PH:
                last_i = ph.pairs // 2 - 1
                if ph.name in ("out1", "out2"):
                    for stage in range(4):
                        leave(stage, *before)
                    before = None
                    dve.wait_ge(bank_free, ph.pair0)
                if ph.name == "out1":
                    dve.wait_ge(tables_loaded, 16 * (len(tables) - 1))
                    dve.wait_ge(poolw_loaded, POOLW_LOADS)
                    step(nc.vector.memset(levels[:, :, 0:PAD], 0.0))
                    for t in range(3):
                        conv_pair(t)
                    for t in range(6):
                        pool_tile(t)
                    pool_out()
                    attention(units1)
                if ph.name == "out2":
                    dve.wait_ge(lam_loaded, 16)
                    step(nc.vector.tensor_tensor(lam[:, 0:4:2, :], lam[:, 0:4:2, :], lam[:, 1:4:2, :], ALU.mult))
                    nc.vector.tensor_reduce(lam_sum[:], lam[:, 0:4:2, :], AX.X, ALU.add).then_inc(lam_ready, 1)
                    step(nc.vector.tensor_scalar(sg[:], sg[:], 1.0 - LAM_INIT, None, ALU.mult))
                    dve.wait_ge(lam_exp_ready, 1)
                    step(nc.vector.tensor_tensor(neg_lam[:], lam_sum[:, 1:2], lam_sum[:, 0:1], ALU.subtract))
                    step(nc.vector.tensor_scalar(neg_lam[:], neg_lam[:], -LAM_INIT, None, ALU.add))
                    for g in range(4):
                        rope_group(g, 4 * g, ROT_A, ropea, ROT_A // 2)
                    for g in range(4):
                        rope_group(4 + g, 24 + 4 * g, P, ropeb, ROT_B // 2)
                    attention(units2)
                slot(ph, 0, 0, before)
                if ph.kind in ("res", "res2", "last"):
                    nc.vector.memset(ssum_g[:], 0.0)
                    step(nc.vector.memset(ssum[:], 0.0))
                if ph.name == "kv":
                    for i in range(last_i):
                        slot(ph, i, 1, (ph, i, 0))
                        slot(ph, i + 1, 0, (ph, i, 1))
                else:
                    slot(ph, 0, 1, (ph, 0, 0))
                    slot(ph, 1, 0, (ph, 0, 1))
                    first, per = 1, {"res": 2, "last": 2, "ffn": 2, "res2": 4}.get(ph.kind, 0)
                    if ph.name == "in2":
                        first = 1 + KT // 4
                        with dve.Fori(1, first) as i:
                            chain.enter(i, 1, 2)
                            for a in range(2):
                                slot(ph, i + a, 1 - a, (ph, i, a))
                                scale_x(2 * i - 2 + a)
                        chain.leave(1, first, 2)
                    with dve.Fori(first, last_i) as i:
                        chain.enter(i, first, per)
                        slot(ph, i, 1, (ph, i, 0))
                        slot(ph, i + 1, 0, (ph, i, 1))
                    chain.leave(first, last_i, per)
                slot(ph, last_i, 1, (ph, last_i, 0))
                before = (ph, last_i, 1)
            leave(0, *before)
            leave(1, *before)
            reciprocal_root(NORMS + 1, r[:])
            for t in range(KT):
                last = nc.vector.scalar_tensor_tensor(x[:, t, :], x[:, t, :], gain[:, N_FINAL, t:t + 1], r[:], ALU.mult, ALU.mult)
                if t % 4 == 3:
                    last.then_inc(xs_ready, 1)


def shape_tables():
    i, j = np.arange(S)[:, None], np.arange(S)[None, :]
    d = i - j
    count = (np.abs(d) <= 64).astype(np.float64) + (d % 4 == 0) + (d % 16 == 0)
    logc = np.where(count > 0, np.log(np.maximum(count, 1)), -1e30).astype(np.float32)
    logc = np.ascontiguousarray(logc.reshape(2, P, S).transpose(1, 0, 2))

    def rope(rot, rows, period):
        f = np.float32
        inv = (f(500000.0) ** (-np.arange(0, rot, 2, dtype=f) / f(rot))).astype(f)
        ang = (np.arange(S, dtype=f)[:, None] * inv[None, :]).astype(f)
        c, s = np.cos(ang).T, np.sin(ang).T
        out = np.zeros((rows, 2, S), f)
        out[:, 0, :] = 1.0
        for o in range(0, rows, period):
            out[o:o + rot, 0] = np.concatenate([c, c])
            out[o:o + rot, 1] = np.concatenate([-s, s])
        return out

    t = np.arange(S, dtype=np.float32)
    inv = np.stack([np.float32(1.0) / np.minimum(t + 1, np.float32(w)) for w in WINDOWS]).astype(np.float32)
    invcnt = np.ascontiguousarray(np.broadcast_to(inv, (P, 4, S)))
    return {"ident_c": np.eye(P, dtype=np.float32), "logc_c": logc, "ropea_c": rope(ROT_A, ROT_A, ROT_A),
            "ropeb_c": rope(ROT_B, P, 64), "invcnt_c": invcnt}


def kernel(**inputs):
    import concourse.bacc as _bacc
    from concourse.bass_utils import run_bass_kernel_spmd as _run

    a = {k: np.asarray(v) for k, v in inputs.items()}

    def per_partition(w, tiles):
        w = w.reshape(w.shape[:-1] + (tiles, P))
        return np.ascontiguousarray(np.moveaxis(w, -1, 0))

    given = {"xT": np.ascontiguousarray(a["x"][0].T), "memT": np.ascontiguousarray(a["mem"][0].T)}
    for name in ("w_kv", "w_in", "w_out", "w_up", "w_down", "w_in_2", "w_out_2", "w_up_2", "w_gate_2", "w_down_2"):
        given[name] = np.ascontiguousarray(a[name][0])
    given["gains"] = per_partition(np.stack([a["g_mix"][0], a["g_mem"][0], a["g_ffn"][0], a["g_final"],
                                             a["norm_attn_2"][0], a["norm_ffn_2"][0], a["norm_final_2"]]), KT)
    given["conv_w"] = per_partition(a["conv_w"][0], 6)
    given["pool_w"] = np.ascontiguousarray(a["pool_w"][0])
    given["pool_scale"] = per_partition(a["pool_scale"][0], 6)
    given["ffn_conv_w"] = per_partition(a["ffn_conv_w"][0], 2 * FT)
    given["ffn_conv_b"] = per_partition(a["ffn_conv_b"][0], 2 * FT)
    given["lambda_qk"] = np.ascontiguousarray(a["lambda_qk_2"][0])
    given["subln"] = per_partition(a["subln_2"][0], 1)
    given.update(shape_tables())

    nc = _bacc.Bacc("TRN2", target_bir_lowering=False, num_devices=1, dynamic_dma_scratch_size=8192)
    args = {n: nc.dram_tensor("in_" + n, v.shape, mybir.dt.from_np(v.dtype), kind="ExternalInput").ap() for n, v in given.items()}
    args["outT"] = nc.dram_tensor("outT", (D, S), F32, kind="ExternalOutput").ap()
    build(nc, **args)
    res = _run(nc, [{"in_" + n: v for n, v in given.items()}], core_ids=[0])
    return np.ascontiguousarray(res.results[0]["outT"].T)[None]
```
